# Optimizing a Trainium2 kernel written in Bass

```python
import math
import jax
import jax.numpy as jnp
from jax import lax
import numpy as np
import jax, jax.numpy as jnp

D_MODEL = 1024
BATCH = 1
SEQ = 256
DEPTH = 4

CHUNK = 64
N_MIXERS = 3
HEAD_DIM = 64
N_HEADS = D_MODEL // HEAD_DIM
D_FF = -(-8 * D_MODEL // (3 * 256)) * 256
RMS_EPS = 1e-6
ROPE_THETA = 10000.0
RW_DECAY_LORA = max(32, int(round(1.8 * D_MODEL ** 0.5 / 32)) * 32)
RW_AAA_LORA = max(32, int(round(1.8 * D_MODEL ** 0.5 / 32)) * 32)
RW_MV_LORA = max(32, int(round(1.3 * D_MODEL ** 0.5 / 32)) * 32)
RW_GATE_LORA = max(32, int(round(0.6 * D_MODEL ** 0.8 / 32)) * 32)
RW_GN_EPS = HEAD_DIM * 1e-5
SB_QBLOCK = 128
DS_TOPK_MAX = 256
DS_IDX_HEADS = 8
DS_IDX_DIM = 64
DS_QBLOCK = CHUNK
DS_IN_WIDTH = 3 * D_MODEL + DS_IDX_HEADS * DS_IDX_DIM + DS_IDX_DIM + DS_IDX_HEADS
N_RWKV = (DEPTH + 2) // 3
N_SB = (DEPTH + 1) // 3
N_DSA = DEPTH // 3


def rms_norm(x, g):
    xf = x.astype(jnp.float32)
    y = xf * lax.rsqrt(jnp.mean(xf * xf, axis=-1, keepdims=True) + RMS_EPS)
    return (y * g.astype(jnp.float32)).astype(x.dtype)

def rope(x, pos):
    half = x.shape[-1] // 2
    inv = 1.0 / (ROPE_THETA ** (jnp.arange(half, dtype=jnp.float32) / half))
    ang = pos.astype(jnp.float32)[:, None] * inv[None, :]
    cos = jnp.cos(ang)[None, :, None, :]
    sin = jnp.sin(ang)[None, :, None, :]
    xf = x.astype(jnp.float32)
    x1, x2 = xf[..., :half], xf[..., half:]
    return jnp.concatenate([x1 * cos - x2 * sin, x1 * sin + x2 * cos], axis=-1).astype(x.dtype)

def swiglu(h, w_gu, w_down):
    g, u = jnp.split(h @ w_gu, 2, axis=-1)
    return (jax.nn.silu(g) * u) @ w_down

def rwkv7_time_mix(h, v_first, mix, w_rkv, w0, w1, w2, a0, a1, a2, g1, g2, k_k, k_a, r_k, ln_w, ln_b, w_out, v_res):
    B, S, D = h.shape
    f32 = jnp.float32
    shifted = jnp.pad(h, ((0, 0), (1, 0), (0, 0)))[:, :-1]
    xm = h[:, :, None, :] + (shifted - h)[:, :, None, :] * mix
    rkv = jnp.einsum('bsjd,jde->bsje', xm[:, :, :3], w_rkv)
    r, k, v = rkv[:, :, 0], rkv[:, :, 1], rkv[:, :, 2]
    xv, xw, xa, xg = xm[:, :, 2], xm[:, :, 3], xm[:, :, 4], xm[:, :, 5]
    logw = -jax.nn.softplus(-(w0 + jnp.tanh(xw @ w1) @ w2).astype(f32)) - 0.5
    decay = jnp.exp(-jnp.exp(logw))
    a = jax.nn.sigmoid((a0 + (xa @ a1) @ a2).astype(f32))
    g = jax.nn.sigmoid(xg @ g1) @ g2
    v_layer = v
    if v_res is not None:
        v0, v1, v2 = v_res
        v = v + (v_first - v) * jax.nn.sigmoid(v0 + (xv @ v1) @ v2)

    def heads(t):
        return t.astype(f32).reshape(B, S, N_HEADS, HEAD_DIM)

    kk = heads(k * k_k)
    kk = kk * lax.rsqrt(jnp.maximum(jnp.sum(kk * kk, axis=-1, keepdims=True), 1e-24))
    k = k.astype(f32) * (1.0 + (a - 1.0) * k_a)
    rh, kh, vh, wh, ah = heads(r), heads(k), heads(v), heads(decay), heads(a)

    def step(state, inp):
        r_t, w_t, k_t, v_t, kk_t, a_t = inp
        sa = jnp.einsum('bhvk,bhk->bhv', state, kk_t)
        state = (state * w_t[:, :, None, :]
                 - sa[..., None] * (kk_t * a_t)[:, :, None, :]
                 + v_t[..., None] * k_t[:, :, None, :])
        return state, jnp.einsum('bhvk,bhk->bhv', state, r_t)

    def tmaj(t):
        return jnp.moveaxis(t, 1, 0)

    s0 = jnp.zeros((B, N_HEADS, HEAD_DIM, HEAD_DIM), f32)
    _, y = lax.scan(step, s0, (tmaj(rh), tmaj(wh), tmaj(kh), tmaj(vh), tmaj(kk), tmaj(ah)))
    y = jnp.moveaxis(y, 0, 1)
    mu = jnp.mean(y, axis=-1, keepdims=True)
    var = jnp.mean(jnp.square(y - mu), axis=-1, keepdims=True)
    y = ((y - mu) * lax.rsqrt(var + RW_GN_EPS)).reshape(B, S, D) * ln_w + ln_b
    y = y + (jnp.sum(rh * kh * r_k, axis=-1, keepdims=True) * vh).reshape(B, S, D)
    out = (y * g).astype(h.dtype) @ w_out
    return out, v_layer

def stick_breaking_attention(h, w_qkv, w_out):
    B, S, D = h.shape
    f32 = jnp.float32
    qkv = (h @ w_qkv).reshape(B, S, 3, N_HEADS, HEAD_DIM)
    q = qkv[:, :, 0].astype(f32) * HEAD_DIM ** -0.5
    k = qkv[:, :, 1].astype(f32)
    v = qkv[:, :, 2]
    nb = S // SB_QBLOCK
    q_blocks = jnp.moveaxis(q.reshape(B, nb, SB_QBLOCK, N_HEADS, HEAD_DIM), 1, 0)
    kpos = jnp.arange(S)

    def block(args):
        q_b, i = args
        qpos = i * SB_QBLOCK + jnp.arange(SB_QBLOCK)
        earlier = kpos[None, :] < qpos[:, None]
        z = jnp.einsum('bqhd,bshd->bhqs', q_b, k)
        log_1m = jnp.where(earlier, jax.nn.log_sigmoid(-z), 0.0)
        between = lax.cumsum(log_1m, axis=3, reverse=True) - log_1m
        att = jnp.where(earlier, jnp.exp(jax.nn.log_sigmoid(z) + between), 0.0)
        return jnp.einsum('bhqs,bshd->bqhd', att.astype(v.dtype), v)

    o = lax.map(block, (q_blocks, jnp.arange(nb)))
    o = jnp.moveaxis(o, 0, 1).reshape(B, S, D)
    return o @ w_out

def dsa_attention(h, w_in, q_norm, k_norm, w_out):
    B, S, D = h.shape
    f32 = jnp.float32
    pos = jnp.arange(S)
    c3 = 3 * D
    c4 = c3 + DS_IDX_HEADS * DS_IDX_DIM
    c5 = c4 + DS_IDX_DIM
    q, k, v, qi, ki, wi = jnp.split(h @ w_in, [D, 2 * D, c3, c4, c5], axis=-1)
    q = rope(rms_norm(q.reshape(B, S, N_HEADS, HEAD_DIM), q_norm), pos)
    k = rope(rms_norm(k.reshape(B, S, N_HEADS, HEAD_DIM), k_norm), pos)
    v = v.reshape(B, S, N_HEADS, HEAD_DIM)
    qi = rope(qi.reshape(B, S, DS_IDX_HEADS, DS_IDX_DIM), pos)
    ki = rope(ki.reshape(B, S, 1, DS_IDX_DIM), pos)[:, :, 0]
    wi = wi * (DS_IDX_HEADS ** -0.5 * DS_IDX_DIM ** -0.5)
    n_sel = min(DS_TOPK_MAX, S // 4)
    nb = S // DS_QBLOCK

    def blocks(t):
        return jnp.moveaxis(t.reshape(B, nb, DS_QBLOCK, *t.shape[2:]), 1, 0)

    kpos = jnp.arange(S)

    def block(args):
        q_b, qi_b, wi_b, i = args
        qpos = i * DS_QBLOCK + jnp.arange(DS_QBLOCK)
        visible = kpos[None, :] < ((qpos // CHUNK + 1) * CHUNK)[:, None]
        idx = jnp.einsum('bqhd,bsd->bqhs', qi_b, ki)
        score = jnp.einsum('bqh,bqhs->bqs', wi_b, jax.nn.relu(idx)).astype(f32)
        score = jnp.where(visible[None], score, -jnp.inf)
        top_val, top_idx = lax.top_k(score, n_sel)
        valid = top_val > -jnp.inf
        k_sel = jax.vmap(lambda kb, ib: kb[ib])(k, top_idx)
        v_sel = jax.vmap(lambda vb, ib: vb[ib])(v, top_idx)
        logits = jnp.einsum('bqhd,bqkhd->bhqk', q_b, k_sel).astype(f32) * HEAD_DIM ** -0.5
        logits = jnp.where(valid[:, None], logits, -jnp.inf)
        p = jax.nn.softmax(logits, axis=-1)
        return jnp.einsum('bhqk,bqkhd->bqhd', p.astype(v.dtype), v_sel)

    o = lax.map(block, (blocks(q), blocks(qi), blocks(wi), jnp.arange(nb)))
    o = jnp.moveaxis(o, 0, 1).reshape(B, S, D)
    return o @ w_out

def first_inputs(seed: int = 0) -> dict:
    key = jax.random.key(seed)
    ks = iter(jax.random.split(key, 64))
    D, F, H, dh = D_MODEL, D_FF, N_HEADS, HEAD_DIM
    nA, nB, nC = N_RWKV, N_SB, N_DSA
    out_scale = D ** -0.5 / math.sqrt(2 * DEPTH)

    def nrm(shape, scale):
        return jax.random.normal(next(ks), shape, jnp.float32) * scale

    def unif(shape, lo, hi):
        return jax.random.uniform(next(ks), shape, jnp.float32, lo, hi)

    return {
        'x': nrm((BATCH, SEQ, D), 1.0),
        'norm_mix': 1.0 + nrm((DEPTH, D), 0.02),
        'norm_ffn': 1.0 + nrm((DEPTH, D), 0.02),
        'ffn_w_gu': nrm((DEPTH, D, 2 * F), D ** -0.5),
        'ffn_w_down': nrm((DEPTH, F, D), F ** -0.5 / math.sqrt(2 * DEPTH)),
        'rw_mix': unif((nA, 6, D), 0.0, 1.0),
        'rw_w_rkv': nrm((nA, 3, D, D), D ** -0.5),
        'rw_w0': unif((nA, D), -5.0, 1.0),
        'rw_w1': nrm((nA, D, RW_DECAY_LORA), D ** -0.5),
        'rw_w2': nrm((nA, RW_DECAY_LORA, D), 0.1 * RW_DECAY_LORA ** -0.5),
        'rw_a0': nrm((nA, D), 0.1),
        'rw_a1': nrm((nA, D, RW_AAA_LORA), D ** -0.5),
        'rw_a2': nrm((nA, RW_AAA_LORA, D), 0.3 * RW_AAA_LORA ** -0.5),
        'rw_g1': nrm((nA, D, RW_GATE_LORA), D ** -0.5),
        'rw_g2': nrm((nA, RW_GATE_LORA, D), RW_GATE_LORA ** -0.5),
        'rw_v0': 1.0 + nrm((nA - 1, D), 0.1),
        'rw_v1': nrm((nA - 1, D, RW_MV_LORA), D ** -0.5),
        'rw_v2': nrm((nA - 1, RW_MV_LORA, D), 0.3 * RW_MV_LORA ** -0.5),
        'rw_k_k': 0.85 + nrm((nA, D), 0.05),
        'rw_k_a': 1.0 + nrm((nA, D), 0.05),
        'rw_r_k': nrm((nA, H, dh), 0.1),
        'rw_ln_w': 1.0 + nrm((nA, D), 0.02),
        'rw_ln_b': nrm((nA, D), 0.02),
        'rw_w_out': nrm((nA, D, D), out_scale),
        'sb_w_qkv': nrm((nB, D, 3 * D), D ** -0.5),
        'sb_w_out': nrm((nB, D, D), out_scale),
        'ds_w_in': nrm((nC, D, DS_IN_WIDTH), D ** -0.5),
        'ds_q_norm': 1.0 + nrm((nC, dh), 0.02),
        'ds_k_norm': 1.0 + nrm((nC, dh), 0.02),
        'ds_w_out': nrm((nC, D, D), out_scale),
    }

def first_block(x, norm_mix, norm_ffn, ffn_w_gu, ffn_w_down,
              rw_mix, rw_w_rkv, rw_w0, rw_w1, rw_w2, rw_a0, rw_a1, rw_a2, rw_g1, rw_g2,
              rw_v0, rw_v1, rw_v2, rw_k_k, rw_k_a, rw_r_k, rw_ln_w, rw_ln_b, rw_w_out,
              sb_w_qkv, sb_w_out,
              ds_w_in, ds_q_norm, ds_k_norm, ds_w_out):
    v_first = None
    for i in range(DEPTH):
        kind, j = i % N_MIXERS, i // N_MIXERS
        h = rms_norm(x, norm_mix[i])
        if kind == 0:
            v_res = None if j == 0 else (rw_v0[j - 1], rw_v1[j - 1], rw_v2[j - 1])
            y, v_layer = rwkv7_time_mix(h, v_first, rw_mix[j], rw_w_rkv[j], rw_w0[j], rw_w1[j], rw_w2[j],
                                        rw_a0[j], rw_a1[j], rw_a2[j], rw_g1[j], rw_g2[j],
                                        rw_k_k[j], rw_k_a[j], rw_r_k[j], rw_ln_w[j], rw_ln_b[j],
                                        rw_w_out[j], v_res)
            if j == 0:
                v_first = v_layer
        elif kind == 1:
            y = stick_breaking_attention(h, sb_w_qkv[j], sb_w_out[j])
        else:
            y = dsa_attention(h, ds_w_in[j], ds_q_norm[j], ds_k_norm[j], ds_w_out[j])
        x = x + y
        x = x + swiglu(rms_norm(x, norm_ffn[i]), ffn_w_gu[i], ffn_w_down[i])
    return x


DEPTH_2 = 2

N_HEADS_A = 8
N_HEADS_B = 8
D_A = N_HEADS_A * HEAD_DIM
D_B = N_HEADS_B * HEAD_DIM
D_MIX = D_A + D_B
D_IN = 4 * D_A + 4 * D_B
SPLIT_POINTS = (D_A, 2 * D_A, 3 * D_A, 4 * D_A,
                4 * D_A + D_B, 4 * D_A + 2 * D_B, 4 * D_A + 3 * D_B)
DILATED_PATTERNS = ((128, 1), (512, 4), (2048, 16))
MOBA_BLOCK = 256
MOBA_TOPK = 3
MOBA_QCHUNK = 128
ROPE_THETA_2 = 500000.0
ROPE_DIM = HEAD_DIM // 4
NEG_INF = -1e30


def rms_norm_2(x, g):
    x32 = x.astype(jnp.float32)
    y = x32 * lax.rsqrt(jnp.mean(x32 * x32, axis=-1, keepdims=True) + RMS_EPS)
    return (y * g.astype(jnp.float32)).astype(x.dtype)

def rope_tables(positions):
    inv_freq = ROPE_THETA_2 ** (-jnp.arange(0, ROPE_DIM, 2, dtype=jnp.float32) / ROPE_DIM)
    ang = positions.astype(jnp.float32)[:, None, :, None] * inv_freq
    return jnp.cos(ang), jnp.sin(ang)

def apply_partial_rope(t, cos, sin):
    r = ROPE_DIM // 2
    cos = cos.astype(t.dtype)
    sin = sin.astype(t.dtype)
    t1, t2, rest = t[..., :r], t[..., r:ROPE_DIM], t[..., ROPE_DIM:]
    return jnp.concatenate([t1 * cos - t2 * sin, t2 * cos + t1 * sin, rest], axis=-1)

def dilated_pattern(q, k, v, window, dilation):
    B, H, S, hd = q.shape
    n = window // dilation
    span = n * dilation
    s_pad = -(-S // span) * span
    L = s_pad // dilation

    def strided(t):
        t = jnp.pad(t, ((0, 0), (0, 0), (0, s_pad - S), (0, 0)))
        t = t.reshape(B, H, L, dilation, hd).transpose(0, 1, 3, 2, 4)
        return t.reshape(B, H, dilation, L // n, n, hd)

    qb, kb, vb = strided(q), strided(k), strided(v)
    nblk = L // n

    def with_prev(t):
        prev = jnp.pad(t, ((0, 0), (0, 0), (0, 0), (1, 0), (0, 0), (0, 0)))[:, :, :, :-1]
        return jnp.concatenate([prev, t], axis=4)

    kw, vw = with_prev(kb), with_prev(vb)
    s = jnp.einsum('bhrnqd,bhrnkd->bhrnqk', qb, kw,
                   preferred_element_type=jnp.float32) * (hd ** -0.5)
    qi = jnp.arange(n)[:, None]
    kj = jnp.arange(2 * n)[None, :]
    delta = qi + n - kj
    blk = jnp.arange(nblk)[:, None, None]
    valid = (delta >= 0) & (delta <= n) & (blk * n + kj - n >= 0)
    s = jnp.where(valid, s, NEG_INF)
    m = jnp.max(s, axis=-1, keepdims=True)
    p = jnp.exp(s - m)
    denom = jnp.sum(p, axis=-1)
    num = jnp.einsum('bhrnqk,bhrnkd->bhrnqd', p.astype(v.dtype), vw,
                     preferred_element_type=jnp.float32)
    o = num / denom[..., None]
    lse = m[..., 0] + jnp.log(denom)
    o = o.reshape(B, H, dilation, L, hd).transpose(0, 1, 3, 2, 4).reshape(B, H, s_pad, hd)[:, :, :S]
    lse = lse.reshape(B, H, dilation, L).transpose(0, 1, 3, 2).reshape(B, H, s_pad)[:, :, :S]
    return o, lse

def dilated_mixture_attention(q, k, v):
    outs, lses = [], []
    for window, dilation in DILATED_PATTERNS:
        o, lse = dilated_pattern(q, k, v, window, dilation)
        outs.append(o)
        lses.append(lse)
    alpha = jax.nn.softmax(jnp.stack(lses, axis=0), axis=0)
    o = jnp.einsum('pbhs,pbhsd->bhsd', alpha, jnp.stack(outs, axis=0))
    return o.astype(q.dtype)

def moba_attention(q, k, v):
    B, H, S, hd = q.shape
    blk = MOBA_BLOCK
    s_pad = -(-S // blk) * blk
    nb = s_pad // blk
    padw = ((0, 0), (0, 0), (0, s_pad - S), (0, 0))
    q, k, v = jnp.pad(q, padw), jnp.pad(k, padw), jnp.pad(v, padw)
    kb = k.reshape(B, H, nb, blk, hd)
    vb = v.reshape(B, H, nb, blk, hd)
    scale = hd ** -0.5
    topk = min(MOBA_TOPK, nb)

    kmean = jnp.mean(kb.astype(jnp.float32), axis=3)
    gate = jnp.einsum('bhsd,bhnd->bhsn', q.astype(jnp.float32), kmean)
    own = jnp.arange(s_pad) // blk
    past = jnp.arange(nb)[None, :] < own[:, None]
    gate = jnp.where(past, gate, NEG_INF)
    _, sel = lax.top_k(gate, topk)

    qc = MOBA_QCHUNK
    nchunk = s_pad // qc
    q_chunks = q.reshape(B, H, nchunk, qc, hd)
    sel_chunks = sel.reshape(B, H, nchunk, qc, topk)
    hidx = jnp.arange(H)[:, None, None]

    def body(idx):
        b = idx // nchunk
        c = idx % nchunk
        q_c = q_chunks[b][:, c]
        sel_c = sel_chunks[b][:, c]
        kb_b, vb_b = kb[b], vb[b]
        qpos = c * qc + jnp.arange(qc)
        ob = (c * qc) // blk
        k_own = lax.dynamic_index_in_dim(kb_b, ob, axis=1, keepdims=False)
        v_own = lax.dynamic_index_in_dim(vb_b, ob, axis=1, keepdims=False)
        kpos = ob * blk + jnp.arange(blk)
        s_own = jnp.einsum('hqd,hkd->hqk', q_c, k_own,
                           preferred_element_type=jnp.float32) * scale
        s_own = jnp.where(kpos[None, :] <= qpos[:, None], s_own, NEG_INF)
        k_sel = kb_b[hidx, sel_c]
        v_sel = vb_b[hidx, sel_c]
        s_sel = jnp.einsum('hqd,hqnkd->hqnk', q_c, k_sel,
                           preferred_element_type=jnp.float32) * scale
        valid = jnp.arange(topk)[None, :] < jnp.minimum(qpos // blk, topk)[:, None]
        s_sel = jnp.where(valid[None, :, :, None], s_sel, NEG_INF)
        scores = jnp.concatenate([s_own, s_sel.reshape(H, qc, topk * blk)], axis=-1)
        p = jax.nn.softmax(scores, axis=-1)
        p_own = p[..., :blk].astype(v.dtype)
        p_sel = p[..., blk:].reshape(H, qc, topk, blk).astype(v.dtype)
        o = (jnp.einsum('hqk,hkd->hqd', p_own, v_own, preferred_element_type=jnp.float32)
             + jnp.einsum('hqnk,hqnkd->hqd', p_sel, v_sel, preferred_element_type=jnp.float32))
        return o.astype(q.dtype)

    out = lax.map(body, jnp.arange(B * nchunk))
    out = out.reshape(B, nchunk, H, qc, hd).transpose(0, 2, 1, 3, 4).reshape(B, H, s_pad, hd)
    return out[:, :, :S]

def hybrid_layer(x, c, cos, sin, pre_g, post_g, w_ada, b_ada, w_in, w_out):
    B, S, _ = x.shape
    mod = jnp.einsum('bd,de->be', jax.nn.silu(c), w_ada) + b_ada
    shift, scale, gate = jnp.split(mod, 3, axis=-1)
    h = rms_norm_2(x, pre_g) * (1 + scale[:, None, :]) + shift[:, None, :]
    proj = jnp.einsum('bsd,de->bse', h, w_in)
    qa, ka, va, ga, qb, kb, vb, gb = jnp.split(proj, SPLIT_POINTS, axis=-1)

    def heads(t, nh):
        return t.reshape(B, S, nh, HEAD_DIM).transpose(0, 2, 1, 3)

    def merge(t):
        return t.transpose(0, 2, 1, 3).reshape(B, S, -1)

    qa = apply_partial_rope(heads(qa, N_HEADS_A), cos, sin)
    ka = apply_partial_rope(heads(ka, N_HEADS_A), cos, sin)
    qb = apply_partial_rope(heads(qb, N_HEADS_B), cos, sin)
    kb = apply_partial_rope(heads(kb, N_HEADS_B), cos, sin)
    o_a = merge(dilated_mixture_attention(qa, ka, heads(va, N_HEADS_A))) * jax.nn.silu(ga)
    o_b = merge(moba_attention(qb, kb, heads(vb, N_HEADS_B))) * jax.nn.silu(gb)
    y = jnp.einsum('bse,ed->bsd', jnp.concatenate([o_a, o_b], axis=-1), w_out)
    y = rms_norm_2(y, post_g)
    return x + gate[:, None, :] * y

def second_inputs(seed: int = 0) -> dict:
    key = jax.random.key(seed)
    ks = jax.random.split(key, 11)
    x = jax.random.normal(ks[0], (BATCH, SEQ, D_MODEL), jnp.float32)
    c = jax.random.normal(ks[1], (BATCH, D_MODEL), jnp.float32)
    offset = jax.random.randint(ks[2], (BATCH, 1), 0, 4096, dtype=jnp.int32)
    positions = (jnp.arange(SEQ, dtype=jnp.int32)[None, :] + offset).astype(jnp.int32)
    pre_norm_gain = 1.0 + 0.02 * jax.random.normal(ks[3], (DEPTH_2, D_MODEL), jnp.float32)
    post_norm_gain = 1.0 + 0.02 * jax.random.normal(ks[4], (DEPTH_2, D_MODEL), jnp.float32)
    w_ada = jax.random.normal(ks[5], (DEPTH_2, D_MODEL, 3 * D_MODEL), jnp.float32) * D_MODEL ** -0.5
    b_ada = 0.01 * jax.random.normal(ks[6], (DEPTH_2, 3 * D_MODEL), jnp.float32)
    w_in = jax.random.normal(ks[7], (DEPTH_2, D_MODEL, D_IN), jnp.float32) * D_MODEL ** -0.5
    w_out = jax.random.normal(ks[8], (DEPTH_2, D_MIX, D_MODEL), jnp.float32) * D_MIX ** -0.5
    return {"x": x, "c": c, "positions": positions,
            "pre_norm_gain": pre_norm_gain, "post_norm_gain": post_norm_gain,
            "w_ada": w_ada, "b_ada": b_ada, "w_in": w_in, "w_out": w_out}

def second_block(x, c, positions, pre_norm_gain, post_norm_gain, w_ada, b_ada, w_in, w_out):
    cos, sin = rope_tables(positions)
    for layer in range(DEPTH_2):
        x = hybrid_layer(x, c, cos, sin, pre_norm_gain[layer], post_norm_gain[layer],
                         w_ada[layer], b_ada[layer], w_in[layer], w_out[layer])
    return x


def setup_inputs(seed=0):
    out = dict(first_inputs(seed))
    for name, value in second_inputs(seed + 1).items():
        if name != "x":
            out[name + "_2"] = value
    return out


def reference(
    x, norm_mix, norm_ffn, ffn_w_gu, ffn_w_down, rw_mix, rw_w_rkv, rw_w0, rw_w1, rw_w2, rw_a0,
    rw_a1, rw_a2, rw_g1, rw_g2, rw_v0, rw_v1, rw_v2, rw_k_k, rw_k_a, rw_r_k, rw_ln_w, rw_ln_b,
    rw_w_out, sb_w_qkv, sb_w_out, ds_w_in, ds_q_norm, ds_k_norm, ds_w_out, c_2, positions_2,
    pre_norm_gain_2, post_norm_gain_2, w_ada_2, b_ada_2, w_in_2, w_out_2,
):
    x = first_block(
        x, norm_mix, norm_ffn, ffn_w_gu, ffn_w_down, rw_mix, rw_w_rkv, rw_w0, rw_w1, rw_w2,
        rw_a0, rw_a1, rw_a2, rw_g1, rw_g2, rw_v0, rw_v1, rw_v2, rw_k_k, rw_k_a, rw_r_k, rw_ln_w,
        rw_ln_b, rw_w_out, sb_w_qkv, sb_w_out, ds_w_in, ds_q_norm, ds_k_norm, ds_w_out,
    )
    return second_block(
        x, c_2, positions_2, pre_norm_gain_2, post_norm_gain_2, w_ada_2, b_ada_2, w_in_2,
        w_out_2,
    )


_drawn_inputs = setup_inputs


def setup_inputs(seed=0):
    import zlib

    import numpy as np

    out = dict(_drawn_inputs(seed))
    spreads = {}
    factors = {'norm_mix': 2.905,
     'norm_ffn': 3.805,
     'rw_w1': 8.0,
     'rw_w2': 8.0,
     'rw_a0': 3.064,
     'rw_v0': 8.0,
     'rw_v1': 3.494,
     'rw_v2': 3.455,
     'rw_k_k': 5.496,
     'rw_k_a': 3.096,
     'rw_ln_w': 7.155,
     'rw_ln_b': 6.515,
     'ds_q_norm': 8.0,
     'ds_k_norm': 8.0,
     'pre_norm_gain_2': 3.163,
     'post_norm_gain_2': 19.067,
     'b_ada_2': 3.278}
    for name, (base, spread) in spreads.items():
        noise = np.random.default_rng([zlib.crc32(name.encode()), seed]).standard_normal(out[name].shape)
        drawn = base * np.exp(spread * noise) if base else spread * noise
        out[name] = jnp.asarray(drawn.astype(out[name].dtype))
    for name, factor in factors.items():
        out[name] = (out[name] * factor).astype(out[name].dtype)
    return out
```

```python
from contextlib import ExitStack

import numpy as np

import concourse.bass as bass
from concourse import mybir

ALU = mybir.AluOpType
ACT = mybir.ActivationFunctionType
F32 = mybir.dt.float32
I32 = mybir.dt.int32
AX_X = mybir.AxisListType.X

P = 128
D = 1024
S = 256
KD = D // P
FF = 2816
HD = 64
EPS = 1e-6
GN_EPS = HD * 1e-5
NEG = -1e30
GONE = -3e38
RING = 6
SLOT = 2048
NBUF = 15
LEVELS = (2, 4, 8, 16, 32)


def const_table():
    i = np.arange(P)
    s, t = i[:, None], i[None, :]
    same = (s // HD) == (t // HD)
    parts = []

    def add(name, a):
        parts.append((name, np.asarray(a, np.float32)))

    add("ident", s == t)
    add("ones1024", np.full((P, P), 1.0 / D))
    add("bones", same * 1.0)
    add("bavg", same / HD)
    add("ntri", -1.0 * (s >= t))
    add("nones", -np.ones((P, P)))
    add("mU", same & (s < t))
    add("mUi", same & (s <= t))
    add("nm1", -1.0 * ((s // 2 == t // 2) & (s % 2 == 0) & (t % 2 == 1)))
    for m in LEVELS:
        add(f"lv{m}", (s // (2 * m) == t // (2 * m)) & (s % (2 * m) < m) & (t % (2 * m) >= m))
    h = HD // 2
    src = np.where(i % HD < h, i + h, i - h)
    sign = np.where(i % HD < h, -1.0, 1.0)
    R = np.zeros((P, P))
    R[src, i] = sign
    add("rot1", R)
    r = HD // 4 // 2
    R = np.zeros((P, P))
    for o in i:
        d = o % HD
        if d < r:
            R[o + r, o] = -1.0
        elif d < 2 * r:
            R[o - r, o] = 1.0
    add("rot2", R)
    pos = np.arange(S, dtype=np.float32)
    inv = (1.0 / (np.float32(10000.0) ** (np.arange(h, dtype=np.float32) / np.float32(h)))).astype(np.float32)
    ang = (pos[None, :] * inv[i % h][:, None]).astype(np.float32)
    add("cos1", np.cos(ang))
    add("sin1", np.sin(ang))
    inv2 = (np.float32(500000.0) ** (-np.arange(0, 16, 2, dtype=np.float32) / np.float32(16))).astype(np.float32)
    add("inv2", np.where(i % HD < 2 * r, inv2[i % r], 0.0)[:, None])
    strict = (s < t) * 1.0
    add("sbm", np.concatenate([strict, np.ones((P, P)), strict], 1))
    add("sbb", np.concatenate([(1 - strict) * NEG, np.zeros((P, P)), (1 - strict) * NEG], 1))
    q2 = np.arange(S)[:, None]
    k2 = np.arange(S)[None, :]
    dl = q2 - k2
    cnt = ((dl >= 0) & (dl <= 128)) * 1 + ((dl >= 0) & (dl % 4 == 0)) * 1 + ((dl >= 0) & (dl % 16 == 0)) * 1
    dil = np.where(cnt > 0, 8.0 * np.log(np.maximum(cnt, 1)), NEG)
    cau = np.where(dl >= 0, 0.0, NEG)
    vis = np.where(k2 < (q2 // 64 + 1) * 64, 0.0, NEG)
    for name, a in (("dil", dil), ("cau", cau), ("vis", vis)):
        add(name, np.concatenate([a[:P, :P], a[P:, :]], 1))
    add("scan", np.broadcast_to((np.arange(S) % HD != 0) * 1.0, (P, S)))
    off, at = {}, 0
    for name, a in parts:
        off[name] = (at, a.shape[1])
        at += a.shape[1]
    return np.ascontiguousarray(np.concatenate([a for _, a in parts], 1)), off


class Queue:

    def __init__(self, sem):
        self.sem, self.n, self.items, self.seen = sem, 0, [], {}

    def last(self):
        return (self.sem, self.n)

    def wait(self, *tokens):
        for tok in tokens:
            if isinstance(tok, list):
                self.wait(*tok)
            elif tok is not None and self.seen.get(id(tok[0]), 0) < tok[1]:
                self.seen[id(tok[0])] = tok[1]
                self.items.append(("wait", tok[0], tok[1]))

    def do(self, fn):
        self.items.append(("do", fn, None))

    def sig(self, fn, sem=None, by=1):
        if sem is None:
            self.n += 1
            self.items.append(("do", fn, (self.sem, 1)))
            return (self.sem, self.n)
        self.items.append(("do", fn, (sem, by)))

    def step(self, fn, *tokens):
        self.wait(self.last(), *tokens)
        return self.sig(fn)

    def free(self, fn, *tokens):
        self.wait(*tokens)
        return self.sig(fn)

    def play(self, eng):
        for kind, a, b in self.items:
            if kind == "wait":
                eng.wait_ge(a, b)
            else:
                ins = a(eng)
                if b is not None:
                    ins.then_inc(b[0], b[1])


def build(nc, A, out_ap, OFF, NCONST):
    ctx = ExitStack()
    with ctx:
        def sb(name, shape, dt=F32):
            return ctx.enter_context(nc.sbuf_tensor(name, shape, dt))

        def sem(name):
            return ctx.enter_context(nc.semaphore(name))

        X = sb("X", [P, KD, S])
        ring = sb("ring", [P, RING, SLOT])
        CT = sb("CT", [P, NCONST])
        cols = sb("cols", [P, 384])
        BUF = [sb(f"B{i}", [P, 2048]) for i in range(NBUF)]
        rstd = sb("rstd", [P, S])
        sg = sb("sg", [P, 2, S])
        lor = sb("lor", [P, S])
        wc = sb("wc", [P, KD, 4])
        small = sb("small", [P, 128])
        mod = sb("mod", [P, 2, 24])
        PSB = [ctx.enter_context(nc.psum_tensor(f"ps{i}", [P, 512], F32)) for i in range(8)]

        pe, dve, act, pool = (Queue(sem(n)) for n in ("s_pe", "s_dve", "s_act", "s_pool"))
        sp = Queue(sem("s_sp"))
        s_slot = [sem(f"s_w{i}") for i in range(RING)]
        s_in = [sem(f"s_in{i}") for i in range(4)]
        s_out = sem("s_out")

        def C(name, a=0, b=None):
            o, n = OFF[name]
            return CT[:, o + a:o + (n if b is None else b)]

        def FM(i):
            return BUF[i][:, :].rearrange("p (k t) -> p k t", k=KD)

        def TM(i):
            return BUF[i][:, :].rearrange("p (j c) -> p j c", j=2)

        bank_free = [None] * 8
        at = [0]

        def bank():
            i = at[0]
            at[0] = (i + 1) % 8
            assert bank_free[i] != "open"
            pe.wait(bank_free[i])
            bank_free[i] = "open"
            return i

        def done(i, *toks):
            bank_free[i] = list(toks)

        def barrier():
            ends = [q.last() for q in (pe, dve, act, pool)]
            for q in (pe, dve, act, pool):
                q.wait(*[e for e in ends if e[0] is not q.sem])

        def mm(o, l, r, start, stop):
            pe.do(lambda e: e.matmul(o, l, r, start=start, stop=stop, skip_group_check=True))

        def mm_sig(o, l, r, start, stop):
            return pe.sig(lambda e: e.matmul(o, l, r, start=start, stop=stop, skip_group_check=True))

        def tr(o, i_):
            n = i_.shape[0]
            return pe.sig(lambda e: e.transpose(o, i_, C("ident")[0:n, 0:n]))

        def tt(o, a, b, op):
            return lambda e: e.tensor_tensor(o, a, b, op)

        def ts(o, a, s1, s2, op0, op1=None):
            if op1 is None:
                return lambda e: e.tensor_scalar(o, a, s1, None, op0)
            return lambda e: e.tensor_scalar(o, a, s1, s2, op0, op1)

        def stt(o, a, s_, b, op0, op1):
            return lambda e: e.scalar_tensor_tensor(out=o, in0=a, scalar=s_, in1=b, op0=op0, op1=op1)

        def cp(o, a):
            return lambda e: e.tensor_copy(o, a)

        def af(o, a, f, **kw):
            return lambda e: e.activation(o, a, f, **kw)

        slot_n, slot_free, slot_at = [0] * RING, [None] * RING, [0]

        def load(pieces):
            i = slot_at[0]
            slot_at[0] = (i + 1) % RING
            sp.wait(slot_free[i])
            for dst, src in pieces:
                d_ = dst(ring[:, i, :])
                sp.sig((lambda d_, src: lambda e: e.dma_start(d_, src))(d_, src), s_slot[i], 16)
                slot_n[i] += 16
            return i, (s_slot[i], slot_n[i])

        def load_w(view, k0, kn, c0, n):
            i, tok = load([(lambda r: r[:, 0:kn * n].rearrange("p (k n) -> p k n", k=kn),
                            view[:, k0:k0 + kn, c0:c0 + n])])
            return i, ring[:, i, 0:kn * n].rearrange("p (k n) -> p k n", k=kn), tok

        def wview(w):
            return w.rearrange("(k p) n -> p k n", p=P)

        def load_cols(view, kt, c0, n):
            lots = []
            for k0 in range(0, kt, 8):
                kn = min(8, kt - k0)
                lots.append((k0, kn) + load_w(view, k0, kn, c0, n))
            return lots

        def fm_block(view, kt, c0, src, ready, evac, n=256):
            lots = load_cols(view, kt, c0, n)
            b = bank()
            for m in range(n // P):
                for k0, kn, slot, w, tok in lots:
                    pe.wait(tok)
                    for k in range(kn):
                        pe.wait(ready[k0 + k])
                        a = (PSB[b][:, m * S:(m + 1) * S], w[:, k, m * P:(m + 1) * P], src(k0 + k),
                             k0 + k == 0, k0 + k == kt - 1)
                        if k == kn - 1:
                            t = mm_sig(*a)
                        else:
                            mm(*a)
                    slot_free[slot] = t
            done(b, evac(b, t))

        def tm_block(view, c0, src, ready, evac, n=256):
            lots = load_cols(view, KD, c0, n)
            _, _, slot, w, tok = lots[0]
            b = bank()
            pe.wait(tok)
            for j in range(2):
                for k in range(KD):
                    pe.wait(ready[k])
                    t = (mm_sig if k == KD - 1 else mm)(
                        PSB[b][:, j * n:(j + 1) * n], src(k)[:, j * P:(j + 1) * P], w[:, k, 0:n], k == 0, k == KD - 1)
            slot_free[slot] = t
            done(b, evac(b, t))

        def two(ap):
            return ap.rearrange("p (k t) -> p k t", k=2)

        K_ld = (s_in[0], 16)
        sp.sig(lambda e: e.dma_start(CT[:, :], A["const"]), s_in[0], 16)
        xin = TM(0)
        sp.sig(lambda e: e.dma_start(xin, A["x"].rearrange("a (j p) c -> p (a j) c", p=P)), s_in[1], 16)
        rows = [BUF[1][:, 128 * i:128 * i + 128] for i in range(3)]
        COL, n_rows, lds = {}, [0, 0, 0], 0

        def row_load(t, name, src, n):
            nonlocal lds
            r = n_rows[t]
            COL[name] = t * 128 + r
            n_rows[t] += n
            lds += 16
            sp.sig(lambda e: e.dma_start(rows[t][r:r + n, :], src), s_in[2], 16)

        def v2(name):
            return A[name].rearrange("a (k p) -> (a k) p", p=P)

        for nm, n in (("norm_mix", 32), ("norm_ffn", 32), ("rw_w0", 16), ("rw_a0", 16), ("rw_k_k", 16), ("rw_k_a", 16)):
            row_load(0, nm, v2(nm), n)
        row_load(1, "rw_mix", A["rw_mix"].rearrange("a m (k p) -> (a m k) p", p=P), 96)
        row_load(1, "rw_r_k", A["rw_r_k"].rearrange("a (k h) d -> (a k) (h d)", h=2), 16)
        row_load(1, "rw_ln_w", v2("rw_ln_w"), 16)
        row_load(2, "rw_ln_b", v2("rw_ln_b"), 16)
        row_load(2, "rw_v0", v2("rw_v0"), 8)
        for nm, n in (("pre_norm_gain_2", 16), ("post_norm_gain_2", 16), ("b_ada_2", 48), ("c_2", 8)):
            row_load(2, nm, v2(nm), n)
        for nm in ("ds_q_norm", "ds_k_norm"):
            r = n_rows[2]
            COL[nm] = 256 + r
            n_rows[2] += 1
            for hh in range(2):
                lds += 16
                sp.sig((lambda r, hh, nm: lambda e: e.dma_start(rows[2][r:r + 1, hh * 64:hh * 64 + 64], A[nm]))(r, hh, nm),
                       s_in[2], 16)
        pos_i = BUF[2][:, 0:S].bitcast(I32)
        sp.sig(lambda e: e.dma_start(pos_i, A["positions_2"].to_broadcast([P, S])), s_in[3], 16)

        def col(name, k, a=0):
            c = COL[name] + a * KD + k
            return cols[:, c:c + 1]

        pe.wait(K_ld, (s_in[2], lds))
        for q in (dve, act, pool):
            q.wait(K_ld)
        b = bank()
        for t in range(3):
            n = n_rows[t]
            tk = tr(PSB[b][:, t * 128:t * 128 + n], rows[t][0:n, :])
        nc_all = 256 + n_rows[2]
        done(b, dve.step(cp(cols[:, 0:nc_all], PSB[b][:, 0:nc_all]), tk))
        pe.wait((s_in[1], 16))
        for g in range(4):
            b = bank()
            for u in range(4):
                k, j = 2 * g + u // 2, u % 2
                tk = tr(PSB[b][:, u * 128:u * 128 + 128], xin[:, j, k * 128:k * 128 + 128])
            done(b, act.step(af(X[:, 2 * g:2 * g + 2, :], two(PSB[b][:, :]), ACT.Copy), tk))

        ka1 = small[:, 0:16]
        c_ka = COL["rw_k_a"]
        dve.step(ts(ka1, cols[:, c_ka:c_ka + 16], -1.0, 1.0, ALU.mult, ALU.add))
        barrier()

        def rsqrt(b, src, o, floor, op, t):
            done(b, dve.step(ts(o, src, floor, None, op), t))
            t = dve.step(lambda e: e.reciprocal(o, o))
            return act.step(af(o, o, ACT.Sqrt), t)

        def rms_rstd(src_fm, sq):
            b = bank()
            toks = [act.step(af(sq[:, 2 * g:2 * g + 2, :], src_fm[:, 2 * g:2 * g + 2, :], ACT.Square)) if g == 0 else
                    act.free(af(sq[:, 2 * g:2 * g + 2, :], src_fm[:, 2 * g:2 * g + 2, :], ACT.Square)) for g in range(4)]
            for k in range(KD):
                pe.wait(toks[k // 2])
                t = (mm_sig if k == KD - 1 else mm)(PSB[b][:, 0:S], C("ones1024"), sq[:, k, :], k == 0, k == KD - 1)
            return rsqrt(b, PSB[b][:, 0:S], rstd[:, :], EPS, ALU.add, t)

        def rms(src_fm, dst, sq, gain):
            t = rms_rstd(src_fm, sq)
            toks = []
            for k in range(KD):
                f = stt(dst[:, k, :], src_fm[:, k, :], gain(k), rstd[:, :], ALU.mult, ALU.mult)
                toks.append(dve.step(f, t) if k == 0 else dve.free(f))
            return toks

        def add_x(g):
            def evac(b, t):
                xs = X[:, 2 * g:2 * g + 2, :]
                return dve.step(tt(xs, xs, two(PSB[b][:, :]), ALU.add), t)
            return evac

        def out_proj(w, src, ready):
            for g in range(4):
                fm_block(wview(w), KD, g * 256, lambda k: src[:, k, :], ready, add_x(g))

        def ffn(layer):
            barrier()
            h = FM(0)
            hk = rms(X, h, FM(1), lambda k: col("norm_ffn", k, layer))
            hid = [FM(2), FM(3), FM(4)]

            def hs(i):
                return hid[i // 8][:, i % 8, :]

            wg = wview(A["ffn_w_gu"][layer])
            sil = [BUF[5][:, 0:512], BUF[5][:, 512:1024]]
            used = [None, None]
            toks = [None] * 22
            for i in range(11):
                sl = sil[i % 2]

                def ev_g(b, t):
                    return act.step(af(sl, PSB[b][:, :], ACT.Silu), t, used[i % 2])

                fm_block(wg, KD, i * 256, lambda k: h[:, k, :], hk, ev_g)
                st = act.last()

                def ev_u(b, t):
                    o = hid[(2 * i) // 8][:, (2 * i) % 8:(2 * i) % 8 + 2, :]
                    return dve.step(tt(o, two(sl), two(PSB[b][:, :]), ALU.mult), t, st)

                fm_block(wg, KD, FF + i * 256, lambda k: h[:, k, :], hk, ev_u)
                used[i % 2] = toks[2 * i] = toks[2 * i + 1] = dve.last()
            wd = wview(A["ffn_w_down"][layer])
            for g in range(4):
                fm_block(wd, 22, g * 256, hs, toks, add_x(g))

        def to_tm(src, j, dst, k0=0):
            toks = []
            for g in range(2):
                b = bank()
                for u in range(4):
                    t = tr(PSB[b][:, u * 128:u * 128 + 128], src[:, 4 * g + u, j * 128:j * 128 + 128])
                t = act.step(af(dst[:, g * 512:g * 512 + 512], PSB[b][:, :], ACT.Copy), t)
                done(b, t)
                toks.append(t)
            return toks

        def rwkv(layer, n):
            barrier()
            h, d = FM(0), FM(1)
            rms(X, h, d, lambda k: col("norm_mix", k, layer))
            dve.step(tt(d[:, :, 1:S], h[:, :, 0:S - 1], h[:, :, 1:S], ALU.subtract))
            dve.step(ts(d[:, :, 0:1], h[:, :, 0:1], -1.0, None, ALU.mult))
            xmb, xm_free, xm_at = [FM(2), FM(3)], [None, None], [0]

            def mixed(m):
                i = xm_at[0]
                xm_at[0] = 1 - i
                toks = []
                for k in range(KD):
                    f = stt(xmb[i][:, k, :], d[:, k, :], col("rw_mix", k, n * 6 + m), h[:, k, :], ALU.mult, ALU.add)
                    toks.append(dve.step(f, xm_free[i]) if k == 0 else dve.free(f))
                return i, xmb[i], toks

            def full(m, w, dst, extra=None):
                i, xm, ready = mixed(m)
                for g in range(4):
                    def ev(b, t):
                        return act.step(af(dst[:, 2 * g:2 * g + 2, :], two(PSB[b][:, :]), ACT.Copy), t)
                    fm_block(wview(w), KD, g * 256, lambda k: xm[:, k, :], ready, ev)
                if extra:
                    extra(xm, ready)
                xm_free[i] = pe.last()

            def down(w1, rank, xm, ready, evac):
                _, w, slot_tok, slot = None, None, None, None
                slot, w, slot_tok = load_w(wview(w1), 0, KD, 0, rank)
                b = bank()
                pe.wait(slot_tok)
                for m0 in range(0, rank, P):
                    mn = min(P, rank - m0)
                    for k in range(KD):
                        pe.wait(ready[k])
                        t = (mm_sig if k == KD - 1 else mm)(
                            PSB[b][0:mn, (m0 // P) * S:(m0 // P + 1) * S], w[:, k, m0:m0 + mn], xm[:, k, :], k == 0, k == KD - 1)
                slot_free[slot] = t
                done(b, evac(b, t))

            def up(w2, rank, src, ready, evac):
                slot, tok = load([(lambda r: r[0:rank, 0:D], w2)])
                pe.wait(tok, ready)
                for g in range(4):
                    b = bank()
                    for m in range(2):
                        c = g * 256 + m * P
                        t = mm_sig(PSB[b][:, m * S:(m + 1) * S], ring[0:rank, slot, c:c + P], src, True, True)
                    done(b, evac(g, b, t))
                slot_free[slot] = t

            def gate_from(w1, rank, func, w2, bias, dst, a=0):
                def go(xm, ready):
                    def ev(b, t):
                        return act.step(af(lor[0:rank, :], PSB[b][0:rank, 0:S], func), t)
                    down(w1, rank, xm, ready, ev)
                    lt = act.last()

                    def ev2(g, b, t):
                        for m in range(2):
                            f = af(dst[:, 2 * g + m, :], PSB[b][:, m * S:(m + 1) * S], ACT.Sigmoid, bias=col(bias, 2 * g + m, a))
                            r = act.step(f, t)
                        return r
                    up(w2, rank, lor[0:rank, :], lt, ev2)
                return go

            r_, k_, v_, cum, a_ = FM(4), FM(5), FM(13 if n == 0 else 6), FM(7), FM(8)
            full(0, A["rw_w_rkv"][n, 0], r_)
            full(1, A["rw_w_rkv"][n, 1], k_)
            vmix = FM(9)
            full(2, A["rw_w_rkv"][n, 2], v_,
                 gate_from(A["rw_v1"][0], 32, ACT.Copy, A["rw_v2"][0], "rw_v0", vmix) if n else None)

            def only(m, go):
                i, xm, ready = mixed(m)
                go(xm, ready)
                xm_free[i] = pe.last()

            sigd = FM(10)
            only(3, gate_from(A["rw_w1"][n], 64, ACT.Tanh, A["rw_w2"][n], "rw_w0", sigd, n))
            only(4, gate_from(A["rw_a1"][n], 64, ACT.Copy, A["rw_a2"][n], "rw_a0", a_, n))

            def sig_g(xm, ready):
                def ev(b, t):
                    act.step(af(sg[:, 0, :], PSB[b][:, 0:S], ACT.Sigmoid), t)
                    return act.step(af(sg[0:32, 1, :], PSB[b][0:32, S:2 * S], ACT.Sigmoid), t)
                down(A["rw_g1"][n], 160, xm, ready, ev)
            only(5, sig_g)
            barrier()

            if n:
                t1 = FM(2)
                pool.step(tt(t1, FM(13), v_, ALU.subtract))
                pool.step(tt(t1, t1, vmix, ALU.mult))
                pool.step(tt(v_, v_, t1, ALU.add))
            for k in range(KD):
                f = (lambda k: lambda e: e.tensor_tensor_scan(cum[:, k, :], C("scan"), sigd[:, k, :], 0.0, ALU.mult, ALU.add))(k)
                ct = dve.step(f) if k == 0 else dve.free(f)
            W, Wi = FM(1), FM(2 if n == 0 else 3)
            edec = float(np.exp(-0.5))
            t_w = act.step(af(W, cum, ACT.Exp, scale=-edec), ct)
            t_wi = act.step(af(Wi, cum, ACT.Exp, scale=edec), ct)
            kk, sq = FM(0), FM(9)
            for k in range(KD):
                f = ts(kk[:, k, :], k_[:, k, :], col("rw_k_k", k, n), None, ALU.mult)
                kt = dve.step(f) if k == 0 else dve.free(f)
            st = act.step(af(sq, kk, ACT.Square), kt, pool.last())
            pe.wait(st)
            for g in range(4):
                b = bank()
                t = mm_sig(PSB[b][:, :], C("bones"), sq[:, 2 * g:2 * g + 2, :], True, True)
                rn = BUF[10][:, g * 512:g * 512 + 512]
                t = rsqrt(b, PSB[b][:, :], rn, 1e-24, ALU.max, t)
                kg = kk[:, 2 * g:2 * g + 2, :]
                nt = pool.step(tt(kg, kg, two(rn), ALU.mult), t)
            tmp = FM(11)
            for k in range(KD):
                f = ts(tmp[:, k, :], a_[:, k, :], col("rw_k_a", k, n), ka1[:, n * 8 + k:n * 8 + k + 1], ALU.mult, ALU.add)
                dve.step(f) if k == 0 else dve.free(f)
            dve.step(tt(k_, k_, tmp, ALU.mult))
            pool.step(tt(a_, kk, a_, ALU.mult), dve.last())
            term = FM(12)
            for k in range(KD):
                f = stt(term[:, k, :], r_[:, k, :], col("rw_r_k", k, n), k_[:, k, :], ALU.mult, ALU.mult)
                tt_ = dve.step(f) if k == 0 else dve.free(f)
            pe.wait(tt_)
            vt = pool.last()
            for g in range(4):
                b = bank()
                t = mm_sig(PSB[b][:, :], C("bones"), term[:, 2 * g:2 * g + 2, :], True, True)
                done(b, dve.step(tt(term[:, 2 * g:2 * g + 2, :], v_[:, 2 * g:2 * g + 2, :], two(PSB[b][:, :]), ALU.mult), t, vt))
            dve.step(tt(r_, r_, W, ALU.mult), t_w)
            dve.step(tt(k_, k_, Wi, ALU.mult), t_wi)
            pool.step(tt(a_, a_, Wi, ALU.mult), t_wi)
            Pm = FM(7)
            k4 = kk.rearrange("p k (c u) -> p (k c) u", u=HD)
            w4 = W.rearrange("p k (c u) -> p (k c) u", u=HD)
            p4 = Pm.rearrange("p k (c u) -> p (k c) u", u=HD)
            pool.step(tt(p4[:, :, 1:HD], k4[:, :, 1:HD], w4[:, :, 0:HD - 1], ALU.mult), t_w, t_wi)
            pool.step(lambda e: e.tensor_copy(p4[:, :, 0:1], k4[:, :, 0:1]))
            dve.step(lambda e: e.tensor_copy(wc[:, :, :].rearrange("p k c -> p (k c)").unsqueeze(2), w4[:, :, HD - 1:HD]))
            V = TM(9)
            pe.wait(pool.last(), dve.last())
            barrier()
            for j in range(2):
                to_tm(v_, j, V[:, j, :])
            barrier()

            R_, Kp, Bt_ = r_, k_, a_
            Y, Mtb = FM(10), BUF[6][:, :].rearrange("p (a q t) -> p a q t", a=2, q=8)
            kTM, bTM = BUF[0][:, 0:1024], BUF[0][:, 1024:2048]
            pTM = BUF[1][:, 0:1024]
            TPn = BUF[1][:, 1024:2048].rearrange("p (q t) -> p q t", q=8)
            U0, Un = BUF[2][:, 0:1024], BUF[2][:, 1024:2048]
            Sbd = BUF[3][:, 0:1024].rearrange("p (q v) -> p q v", q=8)

            def q4(ap):
                return ap.rearrange("p (q t) -> p q t", q=4)

            def part(bf, i):
                return BUF[bf][:, i * 512:i * 512 + 512]

            T = [part(11, 0), part(11, 1)]
            Tt = [part(11, 2), part(11, 3)]
            XB = [part(14, 0), part(14, 1)]
            Bt = [part(14, 2), part(14, 3)]
            Lk = [part(3, 2), part(3, 3)]

            def bc(name):
                return C(name).unsqueeze(1).to_broadcast([P, 4, P])

            dve.step(lambda e: e.memset(Sbd, 0.0))
            for j in range(2):
                tj = slice(j * P, j * P + P)
                barrier()
                to_tm(Kp, j, kTM)
                to_tm(Bt_, j, bTM)
                to_tm(Pm, j, pTM)
                t_tm = act.last()
                pe.wait(t_tm)
                for qd in range(2):
                    x_read = [None, None]
                    t_T, t_Tt, t_B = [None] * 2, [None] * 2, [None] * 2

                    def gram(par, L, Rr):
                        lo = slice(64 * par, 64 * par + 64)
                        b = bank()
                        for q in range(4):
                            p_ = 4 * qd + q
                            t = (mm_sig if q == 3 else mm)(PSB[b][:, q * P:q * P + P], L[lo, p_, tj], Rr[lo, p_, tj], True, True)
                        return b, t

                    for par in range(2):
                        b, t = gram(par, Bt_, Pm)
                        t = dve.step(tt(q4(Bt[par]), q4(PSB[b][:, :]), bc("mU"), ALU.mult), t, pe.last() if qd else None)
                        done(b, t)
                        t_B[par] = t
                        pool.step(tt(q4(Tt[par]), q4(Bt[par]), bc("nm1"), ALU.mult), t, pe.last() if qd else None)
                        t_Tt[par] = pool.step(tt(q4(Tt[par]), q4(Tt[par]), bc("ident"), ALU.add))
                    for par in range(2):
                        b, t = gram(par, Bt_, R_)
                        done(b, dve.step(tt(Mtb[:, par, 4 * qd:4 * qd + 4, :], q4(PSB[b][:, :]), bc("mUi"), ALU.mult), t))
                        b, t = gram(par, Kp, R_)
                        t_x = dve.step(tt(q4(XB[par]), q4(PSB[b][:, :]), bc("mUi"), ALU.mult), t)
                        done(b, t_x)
                        b, t = gram(par, Kp, Pm)
                        t_l = dve.step(tt(q4(Lk[par]), q4(PSB[b][:, :]), bc("mU"), ALU.mult), t)
                        done(b, t_l)
                    for par in range(2):
                        b = bank()
                        pe.wait(t_Tt[par])
                        for q in range(4):
                            t = tr(PSB[b][:, q * P:q * P + P], Tt[par][:, q * P:q * P + P])
                        t_T[par] = act.step(af(T[par], PSB[b][:, :], ACT.Copy), t)
                        done(b, t_T[par])
                    pe.wait(dve.last())
                    b = bank()
                    for par in range(2):
                        for q in range(4):
                            hd = (2 * (4 * qd + q) + par) * HD
                            t = mm_sig(PSB[b][64 * par:64 * par + 64, q * P:q * P + P], V[:, j, hd:hd + HD],
                                       XB[par][:, q * P:q * P + P], True, True)
                        x_read[par] = t
                    done(b, act.step(af(Y[:, 4 * qd:4 * qd + 4, tj], q4(PSB[b][:, :]), ACT.Copy), t))
                    b = bank()
                    for par in range(2):
                        for q in range(4):
                            hd = (2 * (4 * qd + q) + par) * HD
                            t = mm_sig(PSB[b][:, (par * 4 + q) * HD:(par * 4 + q + 1) * HD], Lk[par][:, q * P:q * P + P],
                                       V[:, j, hd:hd + HD], True, True)
                    for par in range(2):
                        t_g = act.step(af(Lk[par][:, 0:256], PSB[b][:, par * 256:par * 256 + 256], ACT.Copy), t)
                    done(b, t_g)
                    for m in LEVELS:
                        t_bm, t_xs = [None] * 2, [None] * 2
                        for par in range(2):
                            t_bm[par] = pool.step(tt(q4(XB[par]), q4(Bt[par]), bc(f"lv{m}"), ALU.mult), t_B[par], x_read[par])
                        for par in range(2):
                            b = bank()
                            pe.wait(t_bm[par], t_T[par], t_Tt[par])
                            for q in range(4):
                                c = slice(q * P, q * P + P)
                                t = (mm_sig if q == 3 else mm)(PSB[b][:, c], XB[par][:, c], T[par][:, c], True, True)
                            t_xs[par] = act.step(af(XB[par], PSB[b][:, :], ACT.Copy), t)
                            done(b, t_xs[par])
                        for par in range(2):
                            pe.wait(t_xs[par])
                            if m != LEVELS[-1]:
                                b = bank()
                                for q in range(4):
                                    c = slice(q * P, q * P + P)
                                    t = (mm_sig if q == 3 else mm)(PSB[b][:, c], Tt[par][:, c], XB[par][:, c], True, True)
                                t_T[par] = dve.step(tt(T[par], T[par], PSB[b][:, :], ALU.subtract), t)
                                done(b, t_T[par])
                            b = bank()
                            for q in range(4):
                                c = slice(q * P, q * P + P)
                                t = (mm_sig if q == 3 else mm)(PSB[b][:, c], XB[par][:, c], Tt[par][:, c], True, True)
                            x_read[par] = t
                            t_Tt[par] = dve.step(tt(Tt[par], Tt[par], PSB[b][:, :], ALU.subtract), t)
                            done(b, t_Tt[par])
                    pe.wait(t_Tt[0], t_Tt[1], t_g)
                    for par in range(2):
                        b = bank()
                        for q in range(4):
                            t = mm_sig(PSB[b][:, q * HD:q * HD + HD], Tt[par][:, q * P:q * P + P],
                                       Lk[par][:, q * HD:q * HD + HD], True, True)
                        u4 = U0.rearrange("p (q a v) -> p q a v", a=2, v=HD)[:, 4 * qd:4 * qd + 4, par, :]
                        done(b, act.step(af(u4, PSB[b][:, 0:256].rearrange("p (q v) -> p q v", q=4), ACT.Copy, scale=-1.0), t))
                    b = bank()
                    for par in range(2):
                        for q in range(4):
                            hd = (2 * (4 * qd + q) + par) * HD
                            t = mm_sig(PSB[b][64 * par:64 * par + 64, q * P:q * P + P], pTM[:, hd:hd + HD],
                                       Tt[par][:, q * P:q * P + P], True, True)
                    done(b, act.step(af(TPn[:, 4 * qd:4 * qd + 4, :], q4(PSB[b][:, :]), ACT.Copy, scale=-1.0), t))
                t_s = dve.last()
                for half in range(2):
                    c_ = 2 * j + half
                    lo = slice(64 * half, 64 * half + 64)
                    pe.wait(act.last(), t_s)
                    for g in range(2):
                        b = bank()
                        for q in range(4):
                            p_ = 4 * g + q
                            t = mm_sig(PSB[b][lo, q * P:q * P + P], TPn[:, p_, lo], Sbd[:, p_, :], True, True)
                        t_u = dve.step(tt(Un[lo, g * 512:g * 512 + 512], U0[lo, g * 512:g * 512 + 512], PSB[b][lo, :], ALU.add), t, act.last())
                        done(b, t_u)
                    pe.wait(t_u)
                    sb_ = [bank(), bank()]
                    for p_ in range(8):
                        o = PSB[sb_[p_ // 4]][:, (p_ % 4) * P:(p_ % 4) * P + P]
                        cs = slice(p_ * P, p_ * P + P)
                        mm(o, kTM[lo, cs], V[lo, j, cs], True, False)
                        t_d = mm_sig(o, bTM[lo, cs], Un[lo, cs], False, True)
                    yb = bank()
                    for p_ in range(8):
                        mm(PSB[yb][:, p_ * HD:p_ * HD + HD], Sbd[:, p_, :], R_[:, p_, c_ * HD:c_ * HD + HD], True, False)
                        for par in range(2):
                            hd = (2 * p_ + par) * HD
                            t_y = mm_sig(PSB[yb][64 * par:64 * par + 64, p_ * HD:p_ * HD + HD], Un[lo, hd:hd + HD],
                                         Mtb[lo, par, p_, lo], False, True)
                    ys = Y[:, :, c_ * HD:c_ * HD + HD]
                    for g in range(2):
                        for par in range(2):
                            pr = slice(64 * par, 64 * par + 64)
                            sd = Sbd[pr, 4 * g:4 * g + 4, 64 * par:64 * par + 64]
                            pd = q4(PSB[sb_[g]][:, :])[pr, :, 64 * par:64 * par + 64]
                            t_a = dve.step(tt(sd, sd, pd, ALU.add), t_d, t_y)
                        done(sb_[g], t_a)
                    for par in range(2):
                        pr = slice(64 * par, 64 * par + 64)
                        sd = Sbd[pr, :, 64 * par:64 * par + 64]
                        t_s = dve.step(tt(sd, sd, wc[pr, :, c_:c_ + 1].to_broadcast([64, 8, 64]), ALU.mult))
                    done(yb, dve.step(tt(ys, ys, PSB[yb][:, :].rearrange("p (k u) -> p k u", k=8), ALU.add), t_y))
            barrier()
            sq = FM(0)
            slot, tok = load([(lambda r: r[:, 0:D], A["rw_g2"][n][0:128, :]),
                              (lambda r: r[0:32, D:2 * D], A["rw_g2"][n][128:160, :])])
            pe.wait(tok)
            ready = []
            for g in range(4):
                yg = Y[:, 2 * g:2 * g + 2, :]
                b = bank()
                t = mm_sig(PSB[b][:, :], C("bavg"), yg, True, True)
                t = dve.step(tt(yg, yg, two(PSB[b][:, :]), ALU.subtract), t)
                done(b, t)
                t = act.step(af(sq[:, 2 * g:2 * g + 2, :], yg, ACT.Square), t)
                pe.wait(t)
                b = bank()
                t = mm_sig(PSB[b][:, :], C("bavg"), sq[:, 2 * g:2 * g + 2, :], True, True)
                rn = BUF[1][:, g * 512:g * 512 + 512]
                t = rsqrt(b, PSB[b][:, :], rn, GN_EPS, ALU.add, t)
                dve.step(tt(yg, yg, two(rn), ALU.mult), t)
                for m in range(2):
                    k = 2 * g + m
                    dve.step(ts(Y[:, k, :], Y[:, k, :], col("rw_ln_w", k, n), col("rw_ln_b", k, n), ALU.mult, ALU.add))
                dve.step(tt(yg, yg, term[:, 2 * g:2 * g + 2, :], ALU.add))
                b = bank()
                for m in range(2):
                    c = (2 * g + m) * P
                    mm(PSB[b][:, m * S:(m + 1) * S], ring[:, slot, c:c + P], sg[:, 0, :], True, False)
                    t = mm_sig(PSB[b][:, m * S:(m + 1) * S], ring[0:32, slot, D + c:D + c + P], sg[0:32, 1, :], False, True)
                t = dve.step(tt(yg, yg, two(PSB[b][:, :]), ALU.mult), t)
                done(b, t)
                ready += [t, t]
            slot_free[slot] = pe.last()
            out_proj(A["rw_w_out"][n], Y, ready)

        def proj_fm(w, c0, dst, k0, nblk, h, hk, scale=1.0):
            for g in range(nblk):
                def ev(b, t):
                    return act.step(af(dst[:, k0 + 2 * g:k0 + 2 * g + 2, :], two(PSB[b][:, :]), ACT.Copy, scale=scale), t)
                fm_block(w, KD, c0 + g * 256, lambda k: h[:, k, :], hk, ev)

        def proj_tm(w, c0, dst, d0, nblk, h, hk):
            for g in range(nblk):
                def ev(b, t):
                    return act.step(af(dst[:, :, d0 + g * 256:d0 + g * 256 + 256],
                                       PSB[b][:, :].rearrange("p (j c) -> p j c", j=2), ACT.Copy), t)
                tm_block(w, c0 + g * 256, lambda k: h[:, k, :], hk, ev)

        def stickbreak(layer):
            barrier()
            h, q_, k_, V, O = FM(0), FM(1), FM(2), TM(3), FM(4)
            hk = rms(X, h, FM(1), lambda k: col("norm_mix", k, layer))
            w = wview(A["sb_w_qkv"][0])
            barrier()
            proj_fm(w, 0, q_, 0, 4, h, hk, 0.125)
            proj_fm(w, D, k_, 0, 4, h, hk)
            proj_tm(w, 2 * D, V, 0, 4, h, hk)
            barrier()
            sp_ = [BUF[5][:, i * 384:(i + 1) * 384] for i in range(4)]
            e_ = [BUF[6][:, i * 384:(i + 1) * 384] for i in range(4)]
            lg = [BUF[7][:, i * 384:(i + 1) * 384] for i in range(4)]
            at_ = [BUF[8][:, i * 384:(i + 1) * 384] for i in range(4)]
            st = {}

            def scores(hh, b, stop):
                lo = slice(64 * (hh % 2), 64 * (hh % 2) + 64)
                p_ = hh // 2
                mm(PSB[b][:, 0:256], k_[lo, p_, 0:128], q_[lo, p_, :], True, stop)
                return mm_sig(PSB[b][:, 256:384], k_[lo, p_, 128:256], q_[lo, p_, 128:256], True, stop)

            def s0(hh):
                i = hh % 4
                b = bank()
                t = scores(hh, b, True)
                act.step(af(e_[i], PSB[b][:, 0:384], ACT.Abs), t)
                act.step(af(e_[i], e_[i], ACT.Exp, scale=-1.0))
                t = act.step(af(e_[i], e_[i], ACT.Ln, bias=1.0))
                t = dve.step(stt(sp_[i], PSB[b][:, 0:384], 0.0, e_[i], ALU.max, ALU.add), t)
                done(b, t)
                st[hh] = pool.step(tt(sp_[i], sp_[i], C("sbm"), ALU.mult), t)

            def s1(hh):
                i = hh % 4
                lo = slice(64 * (hh % 2), 64 * (hh % 2) + 64)
                p_ = hh // 2
                b = bank()
                pe.wait(st[hh])
                mm(PSB[b][:, 0:256], k_[lo, p_, 0:128], q_[lo, p_, :], True, False)
                mm(PSB[b][:, 0:256], C("ntri"), sp_[i][:, 0:256], False, False)
                mm(PSB[b][:, 128:256], C("nones"), sp_[i][:, 256:384], False, True)
                mm(PSB[b][:, 256:384], k_[lo, p_, 128:256], q_[lo, p_, 128:256], True, False)
                t = mm_sig(PSB[b][:, 256:384], C("ntri"), sp_[i][:, 256:384], False, True)
                t = dve.step(tt(lg[i], PSB[b][:, 0:384], C("sbb"), ALU.add), t)
                done(b, t)
                st[hh] = act.step(af(at_[i], lg[i], ACT.Exp), t)

            def s2(hh):
                if hh % 2:
                    b = bank()
                    for g in (hh - 1, hh):
                        lo = slice(64 * (g % 2), 64 * (g % 2) + 64)
                        pe.wait(st[g])
                        i = g % 4
                        mm(PSB[b][lo, 0:256], V[:, 0, g * HD:g * HD + HD], at_[i][:, 0:256], True, False)
                        t = mm_sig(PSB[b][lo, 128:256], V[:, 1, g * HD:g * HD + HD], at_[i][:, 256:384], False, True)
                    done(b, dve.step(lambda e: e.tensor_copy(O[:, hh // 2, :], PSB[b][:, 0:256]), t))
                    st["o"] = dve.last()
                    act.wait(t)

            for i in range(16 + 2):
                if i < 16:
                    s0(i)
                if 1 <= i <= 16:
                    s1(i - 1)
                if i >= 2:
                    s2(i - 2)
            barrier()
            out_proj(A["sb_w_out"][0], O, [dve.last()] * KD)

        def softmax_attn(q_, k_, V, O, bias):
            lg = [BUF[5][:, i * 384:(i + 1) * 384] for i in range(4)]
            pr = [BUF[6][:, i * 384:(i + 1) * 384] for i in range(4)]
            pT = [BUF[7][:, i * 384:(i + 1) * 384] for i in range(4)]
            mx = [small[:, 32 + 8 * i:34 + 8 * i] for i in range(4)]
            nm = [small[:, 34 + 8 * i:36 + 8 * i] for i in range(4)]
            sm = [small[:, 36 + 8 * i:38 + 8 * i] for i in range(4)]
            rs = [small[:, 38 + 8 * i:40 + 8 * i] for i in range(4)]
            st, pvt = {}, {}
            tiles = ((0, 0, 128), (1, 128, 384))

            def s0(hh):
                i = hh % 4
                lo = slice(64 * (hh % 2), 64 * (hh % 2) + 64)
                p_ = hh // 2
                b = bank()
                mm(PSB[b][:, 0:128], q_[lo, p_, 0:128], k_[lo, p_, 0:128], True, True)
                t = mm_sig(PSB[b][:, 128:384], q_[lo, p_, 128:256], k_[lo, p_, :], True, True)
                t = dve.step(tt(lg[i], PSB[b][:, 0:384], bias(hh), ALU.add), t)
                done(b, t)
                for j, a, z in tiles:
                    f = (lambda j, a, z: lambda e: e.tensor_reduce(mx[i][:, j:j + 1], lg[i][:, a:z], AX_X, ALU.max))(j, a, z)
                    dve.step(f) if j == 0 else dve.free(f)
                t = dve.step(ts(nm[i], mx[i], -0.125, None, ALU.mult))
                for j, a, z in tiles:
                    t2 = act.step(af(pr[i][:, a:z], lg[i][:, a:z], ACT.Exp, scale=0.125, bias=nm[i][:, j:j + 1],
                                     accum_out=sm[i][:, j:j + 1]), t)
                st[hh] = t2

            def s1(hh):
                i = hh % 4
                dve.step(lambda e: e.reciprocal(rs[i], sm[i]), st[hh])
                for j, a, z in tiles:
                    f = ts(pr[i][:, a:z], pr[i][:, a:z], rs[i][:, j:j + 1], None, ALU.mult)
                    t = dve.step(f) if j == 0 else dve.free(f)
                b = bank()
                pe.wait(t)
                for u in range(3):
                    t = tr(PSB[b][:, u * P:u * P + P], pr[i][:, u * P:u * P + P])
                t = act.step(af(pT[i], PSB[b][:, 0:384], ACT.Copy), t)
                done(b, t)
                st[hh] = t

            def s2(hh):
                if hh % 2:
                    b = bank()
                    for g in (hh - 1, hh):
                        i = g % 4
                        lo = slice(64 * (g % 2), 64 * (g % 2) + 64)
                        pe.wait(st[g])
                        mm(PSB[b][lo, 0:256], V[:, 0, g * HD:g * HD + HD], pT[i][:, 0:256], True, False)
                        t = mm_sig(PSB[b][lo, 128:256], V[:, 1, g * HD:g * HD + HD], pT[i][:, 256:384], False, True)
                    done(b, dve.step(lambda e: e.tensor_copy(O[:, hh // 2, :], PSB[b][:, 0:256]), t))
                    act.wait(t)

            for i in range(16 + 2):
                if i < 16:
                    s0(i)
                if 1 <= i <= 16:
                    s1(i - 1)
                if i >= 2:
                    s2(i - 2)

        def rope_tiles(src, k0, nk, rot, cos, sin, tmp):
            def bcn(ap, m):
                return ap.unsqueeze(1).to_broadcast([P, m, S])
            used = dve.last()
            for g in range(0, nk, 2):
                m = min(2, nk - g)
                xs = src[:, k0 + g:k0 + g + m, :]
                b = bank()
                t = mm_sig(PSB[b][:, 0:m * S], C(rot), xs, True, True)
                tw = tmp[:, (g % 4):(g % 4) + m, :]
                t1 = dve.step(tt(tw, PSB[b][:, 0:m * S].rearrange("p (k t) -> p k t", k=m), bcn(sin, m), ALU.mult), t, pool.last())
                done(b, t1)
                pool.step(tt(xs, xs, bcn(cos, m), ALU.mult), t, used)
                pool.step(tt(xs, xs, tw, ALU.add), t1)

        def dsa(layer):
            barrier()
            h, q_, k_, V, O = FM(0), FM(1), FM(2), TM(3), FM(4)
            hk = rms(X, h, FM(1), lambda k: col("norm_mix", k, layer))
            w = wview(A["ds_w_in"][0])
            barrier()
            qi = BUF[8][:, 0:1024].rearrange("p (k t) -> p k t", k=4)
            ki = BUF[8][:, 1024:1280].rearrange("p (k t) -> p k t", k=1)
            wi = small[:, 64:80].rearrange("p (j e) -> p j e", j=2)
            proj_fm(w, 3 * D, qi, 0, 2, h, hk)
            c4, c5 = 3 * D + 512, 3 * D + 576

            def pc(o, n):
                return lambda r: r[:, 0:136 * KD].rearrange("p (k n) -> p k n", k=KD)[:, :, o:o + n]
            slot, tok = load([(pc(0, 64), w[:, :, c4:c5]), (pc(64, 64), w[:, :, c4:c5]), (pc(128, 8), w[:, :, c5:c5 + 8])])
            wk = ring[:, slot, 0:136 * KD].rearrange("p (k n) -> p k n", k=KD)
            b = bank()
            pe.wait(tok)
            for k in range(KD):
                t = (mm_sig if k == KD - 1 else mm)(PSB[b][:, 0:S], wk[:, k, 0:128], h[:, k, :], k == 0, k == KD - 1)
            for j in range(2):
                for k in range(KD):
                    t = (mm_sig if k == KD - 1 else mm)(PSB[b][:, S + 8 * j:S + 8 * j + 8], h[:, k, j * P:j * P + P],
                                                        wk[:, k, 128:136], k == 0, k == KD - 1)
            slot_free[slot] = t
            act.step(af(ki, PSB[b][:, 0:S].unsqueeze(1), ACT.Copy), t)
            done(b, act.step(af(wi, PSB[b][:, S:S + 16].rearrange("p (j e) -> p j e", j=2), ACT.Copy,
                                scale=float(8 ** -0.5 * 64 ** -0.5)), t))
            pe.wait(act.last())
            pool.wait(act.last())
            rope_tiles(qi, 0, 4, "rot1", C("cos1"), C("sin1"), FM(9))
            rope_tiles(ki, 0, 1, "rot1", C("cos1"), C("sin1"), FM(9))
            t_idx = pool.last()
            pe.wait(t_idx)
            score, relu = BUF[10][:, 0:384], [BUF[10][:, 384:768], BUF[10][:, 768:1152]]
            work = BUF[10][:, 1152:1536]
            dsb = BUF[10][:, 1536:1920]
            top = small[:, 80:88]
            t_sc = dve.step(lambda e: e.memset(score, 0.0))
            rel_free = [None, None]
            idxb = {}

            def idx_mm(e_):
                lo = slice(64 * (e_ % 2), 64 * (e_ % 2) + 64)
                b = bank()
                mm(PSB[b][:, 0:128], qi[lo, e_ // 2, 0:128], ki[lo, 0, 0:128], True, True)
                t = mm_sig(PSB[b][:, 128:384], qi[lo, e_ // 2, 128:256], ki[lo, 0, :], True, True)
                r_ = relu[e_ % 2]
                t = act.step(af(r_, PSB[b][:, 0:384], ACT.Relu), t, rel_free[e_ % 2])
                done(b, t)
                for j, a, z in ((0, 0, 128), (1, 128, 384)):
                    t2 = dve.step(stt(score[:, a:z], r_[:, a:z], wi[:, j, e_:e_ + 1], score[:, a:z], ALU.mult, ALU.add), t)
                rel_free[e_ % 2] = t2
            for e_ in range(8):
                idx_mm(e_)
            dve.step(tt(score, score, C("vis"), ALU.add))
            for a, z in ((0, 128), (128, 384)):
                cur = score
                for r_ in range(8):
                    dve.step((lambda a, z, cur: lambda e: e.max(top, cur[:, a:z]))(a, z, cur))
                    nxt = work if cur is score else score
                    dve.step((lambda a, z, cur, nxt: lambda e: e.match_replace(nxt[:, a:z], top, cur[:, a:z], GONE))(a, z, cur, nxt))
                    cur = nxt
                dve.step(ts(dsb[:, a:z], cur[:, a:z], -2e38, NEG, ALU.is_gt, ALU.mult))
            for which, dst, gain in ((0, q_, "ds_q_norm"), (1, k_, "ds_k_norm")):
                gcol = cols[:, COL[gain]:COL[gain] + 1]
                for g in range(4):
                    xs = dst[:, 2 * g:2 * g + 2, :]
                    sq = FM(9)[:, 2 * (g % 2):2 * (g % 2) + 2, :]
                    rn = FM(9)[:, 4 + 2 * (g % 2):6 + 2 * (g % 2), :]

                    def ev(b, t):
                        t1 = act.step(af(xs, two(PSB[b][:, :]), ACT.Copy), t)
                        return t1
                    fm_block(w, KD, which * D + g * 256, lambda k: h[:, k, :], hk, ev)
                    t = act.step(af(sq, xs, ACT.Square), pe.last())
                    b = bank()
                    pe.wait(t)
                    t = mm_sig(PSB[b][:, :], C("bavg"), sq, True, True)
                    t = rsqrt(b, two(PSB[b][:, :]), rn, EPS, ALU.add, t)
                    dve.step(stt(xs, xs, gcol, rn, ALU.mult, ALU.mult), t)
            proj_tm(w, 2 * D, V, 0, 4, h, hk)
            barrier()
            rope_tiles(q_, 0, 8, "rot1", C("cos1"), C("sin1"), FM(9))
            rope_tiles(k_, 0, 8, "rot1", C("cos1"), C("sin1"), FM(9))
            barrier()
            softmax_attn(q_, k_, V, O, lambda hh: dsb)
            barrier()
            out_proj(A["ds_w_out"][0], O, [dve.last()] * KD)

        cos2, sin2 = BUF[11][:, 0:256], BUF[11][:, 256:512]

        def rope2_tables():
            pos_f, ang, rr, kf = (BUF[12][:, i * 256:i * 256 + 256] for i in range(4))
            u, v = (BUF[12][:, i * 256:i * 256 + 256] for i in range(4, 6))
            MAGIC = 12582912.0
            two_pi = 2.0 * np.pi
            c1 = float(np.float32(6.28125))
            c2 = float(np.float32(two_pi - 6.28125))
            c2 = float(np.float32(np.round(c2 * 2 ** 20) / 2 ** 20))
            c3 = float(np.float32(two_pi - 6.28125 - c2))
            dve.step(lambda e: e.tensor_copy(pos_f, pos_i), (s_in[3], 16))
            dve.step(ts(ang, pos_f, C("inv2"), None, ALU.mult))
            dve.step(ts(kf, ang, float(1.0 / two_pi), MAGIC, ALU.mult, ALU.add))
            dve.step(ts(kf, kf, -MAGIC, None, ALU.add))
            dve.step(stt(rr, kf, -c1, ang, ALU.mult, ALU.add))
            dve.step(stt(rr, kf, -c2, rr, ALU.mult, ALU.add))
            dve.step(stt(rr, kf, -c3, rr, ALU.mult, ALU.add))
            PI = 3.1415925
            dve.step(ts(rr, rr, PI, -PI, ALU.min, ALU.max))
            dve.step(ts(u, rr, -1.0, None, ALU.mult))
            dve.step(tt(u, u, rr, ALU.max))
            t = dve.step(ts(v, u, -1.0, float(np.pi / 2), ALU.mult, ALU.add))
            act.step(af(sin2, rr, ACT.Sin), t)
            act.step(af(cos2, v, ACT.Sin), t)

        def ada():
            b = bank()
            c_ = COL["c_2"]
            sc = small[:, 16:24]
            t = act.step(af(sc, cols[:, c_:c_ + 8], ACT.Silu))
            pe.wait(t)
            for layer in range(2):
                w = wview(A["w_ada_2"][layer])
                for g in range(12):
                    _, _, slot, wt, tok = load_cols(w, KD, g * 256, 256)[0]
                    pe.wait(tok)
                    for m in range(2):
                        o = layer * 24 + 2 * g + m
                        for k in range(KD):
                            t = (mm_sig if k == KD - 1 else mm)(PSB[b][:, o:o + 1], wt[:, k, m * P:m * P + P], sc[:, k:k + 1],
                                                                k == 0, k == KD - 1)
                    slot_free[slot] = t
            c_b = COL["b_ada_2"]
            done(b, dve.step(tt(mod[:, :, :], PSB[b][:, 0:48].rearrange("p (l e) -> p l e", l=2),
                                cols[:, c_b:c_b + 48].rearrange("p (l e) -> p l e", l=2), ALU.add), t))

        def hybrid(layer):
            barrier()
            h, q_, k_, V, O = FM(0), FM(1), FM(2), TM(3), FM(4)
            G = FM(8)
            gp = small[:, 24:32]
            c_ = COL["pre_norm_gain_2"] + layer * 8
            dve.step(stt(gp, mod[:, layer, 8:16], 1.0, cols[:, c_:c_ + 8], ALU.add, ALU.mult))
            rms(X, h, FM(1), lambda k: gp[:, k:k + 1])
            hk = []
            for k in range(KD):
                f = ts(h[:, k, :], h[:, k, :], mod[:, layer, k:k + 1], None, ALU.add)
                hk.append(dve.step(f) if k == 0 else dve.free(f))
            w = wview(A["w_in_2"][layer])
            barrier()
            for half in range(2):
                c0 = half * 2048
                proj_fm(w, c0, q_, 4 * half, 2, h, hk)
                proj_fm(w, c0 + 512, k_, 4 * half, 2, h, hk)
                proj_tm(w, c0 + 1024, V, 512 * half, 2, h, hk)
                for g in range(2):
                    def ev(b, t):
                        return act.step(af(G[:, 4 * half + 2 * g:4 * half + 2 * g + 2, :], two(PSB[b][:, :]), ACT.Silu), t)
                    fm_block(w, KD, c0 + 1536 + g * 256, lambda k: h[:, k, :], hk, ev)
            barrier()
            rope_tiles(q_, 0, 8, "rot2", cos2, sin2, FM(9))
            rope_tiles(k_, 0, 8, "rot2", cos2, sin2, FM(9))
            barrier()
            softmax_attn(q_, k_, V, O, lambda hh: C("dil") if hh < 8 else C("cau"))
            barrier()
            ot = dve.step(tt(O, O, G, ALU.mult))
            y = FM(1)
            for g in range(4):
                def ev(b, t):
                    return act.step(af(y[:, 2 * g:2 * g + 2, :], two(PSB[b][:, :]), ACT.Copy), t)
                fm_block(wview(A["w_out_2"][layer]), KD, g * 256, lambda k: O[:, k, :], [ot] * KD, ev)
            barrier()
            z = FM(0)
            c_ = COL["post_norm_gain_2"] + layer * 8
            dve.step(tt(gp, mod[:, layer, 16:24], cols[:, c_:c_ + 8], ALU.mult))
            rms(y, z, FM(2), lambda k: gp[:, k:k + 1])
            dve.step(tt(X[:, :, :], X[:, :, :], z, ALU.add))

        rope2_tables_at = 1
        rwkv_first = True
        rope_keep = sb("rope_keep", [P, 2, S])
        cos2, sin2 = rope_keep[:, 0, :], rope_keep[:, 1, :]
        rope2_tables()
        rwkv(0, 0)
        ffn(0)
        stickbreak(1)
        ffn(1)
        dsa(2)
        ffn(2)
        rwkv(3, 1)
        ffn(3)
        ada()
        hybrid(0)
        hybrid(1)
        barrier()
        xo = TM(0)
        for g in range(2):
            for j in range(2):
                b = bank()
                for u in range(4):
                    k = 4 * g + u
                    t = tr(PSB[b][:, u * P:u * P + P], X[:, k, j * P:j * P + P])
                done(b, act.step(af(xo[:, j, g * 512:g * 512 + 512], PSB[b][:, :], ACT.Copy), t))
        sp.wait(act.last())
        sp.sig(lambda e: e.dma_start(out_ap.rearrange("a (j p) c -> p (a j) c", p=P), xo), s_out, 16)
        sp.wait((s_out, 16))

        block = ctx.enter_context(nc.Block())

        @block.sync
        def _(e):
            sp.play(e)

        @block.tensor
        def _(e):
            pe.play(e)

        @block.vector
        def _(e):
            dve.play(e)

        @block.scalar
        def _(e):
            act.play(e)

        @block.gpsimd
        def _(e):
            pool.play(e)


_INS = ["x", "norm_mix", "norm_ffn", "ffn_w_gu", "ffn_w_down", "rw_mix", "rw_w_rkv", "rw_w0", "rw_w1", "rw_w2", "rw_a0",
        "rw_a1", "rw_a2", "rw_g1", "rw_g2", "rw_v0", "rw_v1", "rw_v2", "rw_k_k", "rw_k_a", "rw_r_k", "rw_ln_w", "rw_ln_b",
        "rw_w_out", "sb_w_qkv", "sb_w_out", "ds_w_in", "ds_q_norm", "ds_k_norm", "ds_w_out", "c_2", "positions_2",
        "pre_norm_gain_2", "post_norm_gain_2", "w_ada_2", "b_ada_2", "w_in_2", "w_out_2"]


def kernel(**inputs):
    import numpy as _np
    import concourse.bacc as _bacc
    from concourse import mybir as _mybir
    from concourse.bass_utils import run_bass_kernel_spmd as _run

    nc = _bacc.Bacc("TRN2", target_bir_lowering=False, num_devices=1)
    arrays, aps = {}, {}
    table, off = const_table()
    for name in _INS + ["const"]:
        a = table if name == "const" else _np.ascontiguousarray(inputs[name])
        arrays[f"in_{name}_dram"] = a
        aps[name] = nc.dram_tensor(f"in_{name}_dram", a.shape, _mybir.dt.from_np(a.dtype), kind="ExternalInput").ap()
    out = nc.dram_tensor("out_0_dram", (1, 256, 1024), _mybir.dt.float32, kind="ExternalOutput").ap()
    build(nc, aps, out, off, table.shape[1])
    r = _run(nc, [arrays], core_ids=[0])
    return r.results[0]["out_0_dram"]
```
